# Optimizing a Trainium2 kernel written in Bass

```python
import math
import jax
import jax.numpy as jnp
from jax import lax
import numpy as np

D_MODEL = 1024
BATCH = 1
SEQ = 1024
DEPTH = 1
DEC_BATCH = 8
DEC_SEQ = 8
PAST_LEN = 4096
PAGE_SIZE = 128

HEAD_DIM = 64
N_HEADS_SB = D_MODEL // (2 * HEAD_DIM)
N_HEADS_DIL = D_MODEL // (2 * HEAD_DIM)
SB_WIDTH = N_HEADS_SB * HEAD_DIM
DIL_WIDTH = N_HEADS_DIL * HEAD_DIM
MIX_WIDTH = SB_WIDTH + DIL_WIDTH
D_FF = 4 * D_MODEL
DILATED_PATTERNS = ((128, 1), (512, 4), (2048, 16))
MAX_WINDOW = 2048
Q_BLOCK = 128
SUB_BLOCK = 128
NUM_BUCKETS = 32
MAX_DISTANCE = MAX_WINDOW
RMS_EPS = 1e-6
SB_BIAS_INIT = -5.0
POOL_NUM = 5
POOL_DEN = 4

kernel_name = 'hymba_stickbreak_dilated_decoder_step'

def _rmsnorm(x, g):
    x32 = x.astype(jnp.float32)
    inv = lax.rsqrt(jnp.mean(jnp.square(x32), axis=-1, keepdims=True) + RMS_EPS)
    return (x32 * inv).astype(x.dtype) * g

def _rel_bucket(dist):
    max_exact = NUM_BUCKETS // 2
    d = jnp.maximum(dist, 1).astype(jnp.float32)
    large = max_exact + (jnp.log(d / max_exact) / math.log(MAX_DISTANCE / max_exact)
                         * (NUM_BUCKETS - max_exact)).astype(jnp.int32)
    large = jnp.minimum(large, NUM_BUCKETS - 1)
    return jnp.where(dist < max_exact, dist, large)

def _qkv(x, g, w):
    b, t = x.shape[:2]
    proj = _rmsnorm(x, g) @ w
    cuts = [SB_WIDTH, 2 * SB_WIDTH, 3 * SB_WIDTH,
            3 * SB_WIDTH + DIL_WIDTH, 3 * SB_WIDTH + 2 * DIL_WIDTH]
    qa, ka, va, qb, kb, vb = jnp.split(proj, cuts, axis=-1)
    sb = lambda a: a.reshape(b, t, N_HEADS_SB, HEAD_DIM)
    dl = lambda a: a.reshape(b, t, N_HEADS_DIL, HEAD_DIM)
    return sb(qa), sb(ka), sb(va), dl(qb), dl(kb), dl(vb)

def _sb_attend(q, k, v, mask, sb_bias):
    z = jnp.einsum('bqhd,bkhd->bhqk', q.astype(jnp.float32), k.astype(jnp.float32)) * (q.shape[-1] ** -0.5)
    z = z + sb_bias.astype(jnp.float32)[None, :, None, None]
    log_1m = jnp.where(mask, jax.nn.log_sigmoid(-z), 0.0)
    excl = lax.cumsum(log_1m, axis=3, reverse=True) - log_1m
    a = jnp.where(mask, jnp.exp(jax.nn.log_sigmoid(z) + excl), 0.0)
    return jnp.einsum('bhqk,bkhd->bqhd', a, v.astype(jnp.float32)).astype(q.dtype)

def _sb_prompt(q, k, v, sb_bias):
    b, s, h, hd = q.shape
    nblk = s // Q_BLOCK
    qb = q.reshape(b, nblk, Q_BLOCK, h, hd).transpose(1, 0, 2, 3, 4)
    kpos = jnp.arange(s)

    def one_block(args):
        qi, j = args
        qpos = j * Q_BLOCK + jnp.arange(Q_BLOCK)
        return _sb_attend(qi, k, v, kpos[None, :] < qpos[:, None], sb_bias)

    o = lax.map(one_block, (qb, jnp.arange(nblk)))
    return o.transpose(1, 0, 2, 3, 4).reshape(b, s, h, hd)

def _sb_sample(q, k_new, v_new, k_past, v_past, sb_bias):
    past = k_past.shape[1]
    t = q.shape[1]
    k = jnp.concatenate([k_past, k_new], axis=1)
    v = jnp.concatenate([v_past, v_new], axis=1)
    qpos = past + jnp.arange(t)
    kpos = jnp.arange(past + t)
    return _sb_attend(q, k, v, kpos[None, :] < qpos[:, None], sb_bias)

def _combine_dilations(outs, lses):
    w = jax.nn.softmax(jnp.stack(lses, axis=0), axis=0)
    return jnp.einsum('pbsh,pbshd->bshd', w, jnp.stack(outs, axis=0))

def _dilated_prompt(q, k, v, rel_bias):
    b, s, h, hd = q.shape
    scale = hd ** -0.5
    qi = jnp.arange(SUB_BLOCK)
    ki = jnp.arange(2 * SUB_BLOCK)
    steps = qi[:, None] + SUB_BLOCK - ki[None, :]
    outs, lses = [], []
    for window, dil in DILATED_PATTERNS:
        n_back = window // dil
        ls = s // dil
        nb = -(-ls // SUB_BLOCK)
        lp = nb * SUB_BLOCK

        def to_sub(a):
            a = a.reshape(b, ls, dil, h, hd)
            a = jnp.pad(a, ((0, 0), (0, lp - ls), (0, 0), (0, 0), (0, 0)))
            return a.reshape(b, nb, SUB_BLOCK, dil, h, hd)

        def with_prev(a):
            prev = jnp.pad(a, ((0, 0), (1, 0), (0, 0), (0, 0), (0, 0), (0, 0)))[:, :-1]
            return jnp.concatenate([prev, a], axis=2)

        qs = to_sub(q).astype(jnp.float32)
        kw = with_prev(to_sub(k)).astype(jnp.float32)
        vw = with_prev(to_sub(v)).astype(jnp.float32)
        logits = jnp.einsum('bnqrhd,bnkrhd->bnrhqk', qs, kw) * scale
        bias = rel_bias[_rel_bucket(dil * jnp.clip(steps, 0, n_back))].astype(jnp.float32)
        logits = logits + jnp.transpose(bias, (2, 0, 1))
        key_sub = jnp.arange(nb)[:, None] * SUB_BLOCK + ki[None, :] - SUB_BLOCK
        valid = ((steps >= 0) & (steps <= n_back))[None] & (key_sub >= 0)[:, None, :]
        logits = jnp.where(valid[None, :, None, None], logits, -jnp.inf)
        lse = jax.nn.logsumexp(logits, axis=-1)
        p = jnp.exp(logits - lse[..., None])
        o = jnp.einsum('bnrhqk,bnkrhd->bnqrhd', p, vw)
        outs.append(o.reshape(b, lp, dil, h, hd)[:, :ls].reshape(b, s, h, hd))
        lses.append(jnp.transpose(lse, (0, 1, 4, 2, 3)).reshape(b, lp, dil, h)[:, :ls].reshape(b, s, h))
    return _combine_dilations(outs, lses).astype(q.dtype)

def _dilated_sample(q, k_buf, v_buf, rel_bias):
    t = q.shape[1]
    lb = k_buf.shape[1] - t
    q32 = q.astype(jnp.float32)
    scale = q.shape[-1] ** -0.5
    outs, lses = [], []
    for window, dil in DILATED_PATTERNS:
        m = jnp.arange(window // dil + 1)
        idx = lb + jnp.arange(t)[:, None] - dil * m[None, :]
        valid = idx >= 0
        idx = jnp.maximum(idx, 0)
        kg = jnp.take(k_buf, idx, axis=1).astype(jnp.float32)
        vg = jnp.take(v_buf, idx, axis=1).astype(jnp.float32)
        bias = rel_bias[_rel_bucket(dil * m)].astype(jnp.float32)
        logits = jnp.einsum('bthd,btmhd->bhtm', q32, kg) * scale + bias.T[:, None, :]
        logits = jnp.where(valid[None, None], logits, -jnp.inf)
        lse = jax.nn.logsumexp(logits, axis=-1)
        p = jnp.exp(logits - lse[..., None])
        outs.append(jnp.einsum('bhtm,btmhd->bthd', p, vg))
        lses.append(jnp.transpose(lse, (0, 2, 1)))
    return _combine_dilations(outs, lses).astype(q.dtype)

def _finish(x, o_a, o_b, g_sb, g_dil, w_out, g_mlp, w_up, w_down):
    flat = lambda o: o.reshape(o.shape[:2] + (-1,))
    mixed = jnp.concatenate([_rmsnorm(flat(o_a), g_sb), _rmsnorm(flat(o_b), g_dil)], axis=-1) @ w_out
    x = x + mixed
    hdn = jax.nn.relu(_rmsnorm(x, g_mlp) @ w_up)
    return x + jnp.square(hdn) @ w_down

def setup_inputs(seed: int = 0) -> dict:
    key = jax.random.key(seed)
    ks = jax.random.split(key, 20)
    f32 = jnp.float32
    n_pages = PAST_LEN // PAGE_SIZE
    n_pool = (POOL_NUM * DEC_BATCH * n_pages + POOL_DEN - 1) // POOL_DEN
    win_buf = min(MAX_WINDOW, PAST_LEN)
    nrm = lambda k, shape, s=1.0: jax.random.normal(k, shape, f32) * s
    page_table = jax.random.permutation(ks[6], n_pool)[:DEC_BATCH * n_pages]
    page_table = page_table.reshape(DEC_BATCH, n_pages).astype(jnp.int32)
    return {
        'x_prompt': nrm(ks[0], (BATCH, SEQ, D_MODEL)),
        'x_sample': nrm(ks[1], (DEC_BATCH, DEC_SEQ, D_MODEL)),
        'cache_sb_k': nrm(ks[2], (DEPTH, n_pool, PAGE_SIZE, N_HEADS_SB, HEAD_DIM)),
        'cache_sb_v': nrm(ks[3], (DEPTH, n_pool, PAGE_SIZE, N_HEADS_SB, HEAD_DIM)),
        'cache_win_k': nrm(ks[4], (DEPTH, DEC_BATCH, win_buf, N_HEADS_DIL, HEAD_DIM)),
        'cache_win_v': nrm(ks[5], (DEPTH, DEC_BATCH, win_buf, N_HEADS_DIL, HEAD_DIM)),
        'page_table': page_table,
        'rel_bias': nrm(ks[7], (NUM_BUCKETS, N_HEADS_DIL), 0.3),
        'g_attn': 1.0 + nrm(ks[8], (DEPTH, D_MODEL), 0.02),
        'w_in': nrm(ks[9], (DEPTH, D_MODEL, 3 * SB_WIDTH + 3 * DIL_WIDTH), D_MODEL ** -0.5),
        'sb_bias': SB_BIAS_INIT + nrm(ks[17], (DEPTH, N_HEADS_SB), 0.3),
        'g_out_sb': 1.0 + nrm(ks[10], (DEPTH, SB_WIDTH), 0.02),
        'g_out_dil': 1.0 + nrm(ks[11], (DEPTH, DIL_WIDTH), 0.02),
        'w_out': nrm(ks[12], (DEPTH, MIX_WIDTH, D_MODEL), MIX_WIDTH ** -0.5),
        'g_mlp': 1.0 + nrm(ks[13], (DEPTH, D_MODEL), 0.02),
        'w_up': nrm(ks[14], (DEPTH, D_MODEL, D_FF), D_MODEL ** -0.5),
        'w_down': nrm(ks[15], (DEPTH, D_FF, D_MODEL), D_FF ** -0.5),
        'g_final': 1.0 + nrm(ks[16], (D_MODEL,), 0.02),
    }

def reference(x_prompt, x_sample, cache_sb_k, cache_sb_v, cache_win_k, cache_win_v, page_table,
              rel_bias, g_attn, w_in, sb_bias, g_out_sb, g_out_dil, w_out, g_mlp, w_up, w_down, g_final):
    x = x_prompt
    s = x.shape[1]
    keep_p = max(s - MAX_WINDOW, 0)
    sbk_p, sbv_p, wk_p, wv_p = [], [], [], []
    for l in range(DEPTH):
        qa, ka, va, qb, kb, vb = _qkv(x, g_attn[l], w_in[l])
        o_a = _sb_prompt(qa, ka, va, sb_bias[l])
        o_b = _dilated_prompt(qb, kb, vb, rel_bias)
        x = _finish(x, o_a, o_b, g_out_sb[l], g_out_dil[l], w_out[l], g_mlp[l], w_up[l], w_down[l])
        sbk_p.append(ka)
        sbv_p.append(va)
        wk_p.append(kb[:, keep_p:])
        wv_p.append(vb[:, keep_p:])
    y_prompt = _rmsnorm(x, g_final)

    xs = x_sample
    db, t = xs.shape[:2]
    sbk_s, sbv_s, wk_s, wv_s = [], [], [], []
    for l in range(DEPTH):
        qa, ka, va, qb, kb, vb = _qkv(xs, g_attn[l], w_in[l])
        k_past = jnp.take(cache_sb_k[l], page_table, axis=0).reshape(db, -1, N_HEADS_SB, HEAD_DIM)
        v_past = jnp.take(cache_sb_v[l], page_table, axis=0).reshape(db, -1, N_HEADS_SB, HEAD_DIM)
        o_a = _sb_sample(qa, ka, va, k_past, v_past, sb_bias[l])
        k_buf = jnp.concatenate([cache_win_k[l], kb], axis=1)
        v_buf = jnp.concatenate([cache_win_v[l], vb], axis=1)
        o_b = _dilated_sample(qb, k_buf, v_buf, rel_bias)
        xs = _finish(xs, o_a, o_b, g_out_sb[l], g_out_dil[l], w_out[l], g_mlp[l], w_up[l], w_down[l])
        sbk_s.append(ka)
        sbv_s.append(va)
        wk_s.append(k_buf[:, t:])
        wv_s.append(v_buf[:, t:])
    y_sample = _rmsnorm(xs, g_final)

    return (y_prompt, y_sample,
            jnp.stack(sbk_p, 0), jnp.stack(sbv_p, 0), jnp.stack(sbk_s, 0), jnp.stack(sbv_s, 0),
            jnp.stack(wk_p, 0), jnp.stack(wv_p, 0), jnp.stack(wk_s, 0), jnp.stack(wv_s, 0))


_drawn_inputs = setup_inputs


def setup_inputs(seed=0):
    import zlib

    import numpy as np

    out = dict(_drawn_inputs(seed))
    spreads = {}
    factors = {'g_out_sb': 5.032, 'g_out_dil': 5.141, 'g_mlp': 3.597, 'g_final': 2.848}
    for name, (base, spread) in spreads.items():
        noise = np.random.default_rng([zlib.crc32(name.encode()), seed]).standard_normal(out[name].shape)
        drawn = base * np.exp(spread * noise) if base else spread * noise
        out[name] = jnp.asarray(drawn.astype(out[name].dtype))
    for name, factor in factors.items():
        out[name] = (out[name] * factor).astype(out[name].dtype)
    return out
```

```python
from contextlib import ExitStack

import concourse.bass as bass
from concourse import mybir

F32 = mybir.dt.float32
F32R = mybir.dt.float32r
BF16 = mybir.dt.bfloat16
I32 = mybir.dt.int32
ALU = mybir.AluOpType
ACT = mybir.ActivationFunctionType
AX_X = mybir.AxisListType.X
ds = bass.ds

P = 128
D_MODEL = 1024
KC = D_MODEL // P
SEQ = 1024
B, TS = 8, 8
NS = B * TS
T = SEQ + NS
HEADS, HD = 8, 64
W = HEADS * HD
PAIRS = HEADS // 2
D_FF = 4 * D_MODEL
WIN = 2048
PAGES, PAGE = 32, 128
EPS = 1e-6
SCALE = HD ** -0.5
QT = SEQ // P
DIST0 = WIN + TS - 1
LD = DIST0 + P
BANKS = ((0, 512), (512, 512), (1024, NS))


def load_tokens(nc, cx, x_prompt, x_sample, ident, xT):
    with ExitStack() as st:
        xin = st.enter_context(nc.sbuf_tensor("xin", [P, 2, D_MODEL], F32))
        turned = st.enter_context(nc.psum_tensor("x_turned", [P, 2, D_MODEL], F32))
        loaded = [cx.sem(f"x_loaded{s}") for s in range(2)]
        turn_done, left_out, right_out = cx.sem("x_turn_done"), cx.sem("x_left_out"), cx.sem("x_right_out")
        half = KC // 2
        with nc.Block() as block:
            @block.sync
            def _(sp):
                with sp.Fori(0, QT // 2) as i:
                    for s in range(2):
                        rows = sp.snap(i * 2 * P + s * P)
                        sp.wait_ge(turn_done, i * 2 + s + 1)
                        sp.dma_start(xin[:, s, :], x_prompt[0, ds(rows, P), :]).then_inc(loaded[s], 16)
                sp.wait_ge(turn_done, QT + 1)
                sp.dma_start(xin[0:NS, 0, :], x_sample.rearrange("b t d -> (b t) d")).then_inc(loaded[0], 16)

            @block.tensor
            def _(pe):
                pe.sem_inc(turn_done, 2)

                def turn(s, rows):
                    for c in range(KC):
                        last = pe.transpose(turned[:, s, c * P:c * P + rows], xin[0:rows, s, c * P:(c + 1) * P],
                                            ident[0:rows, 0:rows])
                    last.then_inc(turn_done, 1)

                with pe.Fori(0, QT // 2) as i:
                    for s in range(2):
                        pe.wait_ge(loaded[s], i * 16 + 16)
                        pe.wait_ge(left_out, i * 2 + s + 1)
                        pe.wait_ge(right_out, i * 2 + s + 1)
                        turn(s, P)
                pe.wait_ge(loaded[0], (QT // 2 + 1) * 16)
                pe.wait_ge(left_out, QT + 1)
                pe.wait_ge(right_out, QT + 1)
                turn(0, NS)

            @block.vector
            def _(dve):
                dve.sem_inc(left_out, 2)
                with dve.Fori(0, QT // 2) as i:
                    for s in range(2):
                        dve.wait_ge(turn_done, i * 2 + s + 3)
                        dve.tensor_copy(xT[:, 0:half, ds(i * 2 * P + s * P, P)],
                                        turned[:, s, 0:half * P].rearrange("p (c t) -> p c t", t=P)).then_inc(left_out, 1)
                dve.wait_ge(turn_done, QT + 3)
                dve.tensor_copy(xT[:, 0:half, SEQ:T], turned[:, 0, 0:half * P].rearrange(
                    "p (c t) -> p c t", t=P)[:, :, 0:NS]).then_inc(left_out, 1)

            @block.scalar
            def _(act):
                act.sem_inc(right_out, 2)
                with act.Fori(0, QT // 2) as i:
                    for s in range(2):
                        act.wait_ge(turn_done, i * 2 + s + 3)
                        act.activation(xT[:, half:KC, ds(i * 2 * P + s * P, P)],
                                       turned[:, s, half * P:].rearrange("p (c t) -> p c t", t=P),
                                       ACT.Copy).then_inc(right_out, 1)
                act.wait_ge(turn_done, QT + 3)
                act.activation(xT[:, half:KC, SEQ:T], turned[:, 0, half * P:].rearrange(
                    "p (c t) -> p c t", t=P)[:, :, 0:NS], ACT.Copy).then_inc(right_out, 1)


def rms_stage(nc, cx, tag, src, gain, ones, groups, hi=None, lo=None, plain=None, load=None):
    per = KC // groups
    with ExitStack() as st:
        sq = st.enter_context(nc.sbuf_tensor(f"{tag}_sq", [P, 2, T], F32))
        root = st.enter_context(nc.sbuf_tensor(f"{tag}_root", [P, groups, T], F32))
        rstd = st.enter_context(nc.sbuf_tensor(f"{tag}_rstd", [P, groups, T], F32))
        nrm = st.enter_context(nc.sbuf_tensor(f"{tag}_nrm", [P, 2, T], F32)) if plain is None else None
        total = st.enter_context(nc.psum_tensor(f"{tag}_total", [P, groups, 1536], F32))
        fetched, squared, summed = cx.sem(f"{tag}_fetched"), cx.sem(f"{tag}_squared"), cx.sem(f"{tag}_summed")
        rooted, inverted, normed = cx.sem(f"{tag}_rooted"), cx.sem(f"{tag}_inverted"), cx.sem(f"{tag}_normed")
        hi_done, lo_done = cx.sem(f"{tag}_hi_done"), cx.sem(f"{tag}_lo_done")
        with nc.Block() as block:
            if load is not None:
                @block.sync
                def _(sp):
                    sp.dma_start(src[:, :, :], load.rearrange("(c p) t -> p c t", p=P)).then_inc(fetched, 16)

            @block.scalar
            def _(act):
                if load is not None:
                    act.wait_ge(fetched, 16)
                for c in range(KC):
                    if c >= 2:
                        act.wait_ge(summed, c - 1)
                    act.activation(sq[:, c % 2, :], src[:, c, :], ACT.Square).then_inc(squared, 1)
                for g in range(groups):
                    act.wait_ge(summed, (g + 1) * per)
                    act.activation(root[:, g, :], total[:, g, 0:T], ACT.Sqrt, bias=cx.eps[:, 0:1],
                                   scale=1.0 / (per * P)).then_inc(rooted, 1)
                if plain is None:
                    for c in range(KC):
                        act.wait_ge(normed, c + 1)
                        act.activation(hi[:, c, :], nrm[:, c % 2, :], ACT.Copy).then_inc(hi_done, 1)

            @block.tensor
            def _(pe):
                for c in range(KC):
                    pe.wait_ge(squared, c + 1)
                    for t0, n in BANKS:
                        last = pe.matmul(total[:, c // per, t0:t0 + n], ones[:, :], sq[:, c % 2, t0:t0 + n],
                                         start=(c % per == 0), stop=(c % per == per - 1))
                    last.then_inc(summed, 1)

            @block.vector
            def _(dve):
                if load is not None:
                    dve.wait_ge(fetched, 16)
                for g in range(groups):
                    dve.wait_ge(rooted, g + 1)
                    dve.reciprocal(rstd[:, g, :], root[:, g, :]).then_inc(inverted, 1)

                def low(c):
                    dve.wait_ge(hi_done, c + 1)
                    dve.tensor_tensor(lo[:, c, :], nrm[:, c % 2, :], hi[:, c, :].bitcast(F32),
                                      ALU.subtract).then_inc(lo_done, 1)

                for c in range(KC):
                    if c % per == 0:
                        dve.wait_ge(inverted, c // per + 1)
                    if plain is None and c >= 2:
                        dve.wait_ge(lo_done, c - 1)
                    out = nrm[:, c % 2, :] if plain is None else plain[:, c, :]
                    dve.scalar_tensor_tensor(out=out, in0=src[:, c, :], scalar=gain[:, c:c + 1],
                                             in1=rstd[:, c // per, :], op0=ALU.mult,
                                             op1=ALU.mult).then_inc(normed, 1)
                    if plain is None and c >= 1:
                        low(c - 1)
                if plain is None:
                    low(KC - 1)


def split_products(pe, out, w_hi, w_lo, x_hi, x_lo, k, kn, w_cols):
    for part, (w, x) in enumerate(((w_hi, x_hi), (w_hi, x_lo), (w_lo, x_hi))):
        for t0, n in BANKS:
            last = pe.matmul(out[:, t0:t0 + n], w[:, k, w_cols], x[:, k, t0:t0 + n],
                             start=(k == 0 and part == 0), stop=(k == kn - 1 and part == 2))
    return last


def dense_stage(nc, cx, tag, weights, hi, lo, turns, store=None, residual=None):
    PW = 256
    with ExitStack() as st:
        raw = st.enter_context(nc.sbuf_tensor(f"{tag}_raw", [P, 2, KC, PW], F32))
        w_hi = st.enter_context(nc.sbuf_tensor(f"{tag}_w_hi", [P, 2, KC, PW], F32R))
        w_lo = st.enter_context(nc.sbuf_tensor(f"{tag}_w_lo", [P, 2, KC, PW], F32R))
        out = st.enter_context(nc.sbuf_tensor(f"{tag}_out", [P, 2, T], F32)) if store is not None else None
        acc = st.enter_context(nc.psum_tensor(f"{tag}_acc", [P, 2, 1536], F32))
        fetched = [cx.sem(f"{tag}_fetched{s}") for s in range(2)]
        stored = [cx.sem(f"{tag}_stored{s}") for s in range(2)]
        hi_done, lo_done = cx.sem(f"{tag}_hi_done"), cx.sem(f"{tag}_lo_done")
        acc_done, acc_out = cx.sem(f"{tag}_acc_done"), cx.sem(f"{tag}_acc_out")
        with nc.Block() as block:
            @block.sync
            def _(sp):
                def fetch(i, s, wait):
                    col = i * 2 * PW + s * PW
                    col = col if isinstance(i, int) else sp.snap(col)
                    if wait:
                        sp.wait_ge(lo_done, i * 2 + s - 1)
                    sp.dma_start(raw[:, s, :, :], weights[:, ds(col, PW)].rearrange(
                        "(c p) n -> p c n", p=P)).then_inc(fetched[s], 16)

                def turn(i, more):
                    for s in range(2):
                        if store is not None:
                            for c in range(2):
                                row = i * 4 * P + (s * 2 + c) * P
                                row = row if isinstance(i, int) else sp.snap(row)
                                sp.wait_ge(acc_out, i * 4 + s * 2 + c + 3)
                                sp.dma_start(store[ds(row, P), :], out[:, c, :]).then_inc(stored[c], 16)
                        if more:
                            fetch(i + 1, s, True)

                fetch(0, 0, False)
                fetch(0, 1, False)
                with sp.Fori(0, turns - 1) as i:
                    turn(i, True)
                turn(turns - 1, False)
                if store is not None:
                    for c in range(2):
                        sp.wait_ge(stored[c], turns * 32 + 16)

            @block.scalar
            def _(act):
                with act.Fori(0, turns) as i:
                    for s in range(2):
                        act.wait_ge(fetched[s], i * 16 + 16)
                        act.wait_ge(acc_done, i * 4 + s * 2 + 2)
                        act.activation(w_hi[:, s, :, :], raw[:, s, :, :], ACT.Copy).then_inc(hi_done, 1)

            @block.gpsimd
            def _(pool):
                with pool.Fori(0, turns) as i:
                    for s in range(2):
                        pool.wait_ge(hi_done, i * 2 + s + 1)
                        pool.tensor_tensor(out=w_lo[:, s, :, :], in0=raw[:, s, :, :],
                                           in1=w_hi[:, s, :, :].bitcast(F32), op=ALU.subtract).then_inc(lo_done, 1)

            @block.tensor
            def _(pe):
                pe.sem_inc(acc_done, 4)
                with pe.Fori(0, turns) as i:
                    for s in range(2):
                        pe.wait_ge(lo_done, i * 2 + s + 1)
                        for c in range(2):
                            pe.wait_ge(acc_out, i * 4 + s * 2 + c + 1)
                            for k in range(KC):
                                last = split_products(pe, acc[:, c, :], w_hi[:, s], w_lo[:, s], hi, lo, k, KC,
                                                      slice(c * P, (c + 1) * P))
                            last.then_inc(acc_done, 1)

            @block.vector
            def _(dve):
                dve.sem_inc(acc_out, 2)
                if store is not None:
                    for c in range(2):
                        dve.sem_inc(stored[c], 16)
                with dve.Fori(0, turns) as i:
                    for s in range(2):
                        for c in range(2):
                            dve.wait_ge(acc_done, i * 4 + s * 2 + c + 5)
                            if store is not None:
                                dve.wait_ge(stored[c], i * 32 + s * 16 + 16)
                                dve.tensor_copy(out[:, c, :], acc[:, c, 0:T]).then_inc(acc_out, 1)
                            else:
                                x = residual[:, ds(i * 4 + (s * 2 + c), 1), :].rearrange("p o t -> p (o t)")
                                dve.tensor_tensor(x, x, acc[:, c, 0:T], ALU.add).then_inc(acc_out, 1)


def mlp_stage(nc, cx, w_up, w_down, hi, lo, xT, caches, moved):
    G = 512
    GC = G // P
    turns = D_FF // G
    with ExitStack() as st:
        raw = st.enter_context(nc.sbuf_tensor("mlp_raw", [P, 2, 2048], F32))
        w_hi = st.enter_context(nc.sbuf_tensor("mlp_w_hi", [P, 2, 2048], F32R))
        w_lo = st.enter_context(nc.sbuf_tensor("mlp_w_lo", [P, 2, 2048], F32R))
        act_h = st.enter_context(nc.sbuf_tensor("mlp_h", [P, 2, T], F32))
        h_hi = st.enter_context(nc.sbuf_tensor("mlp_h_hi", [P, GC, T], F32R))
        h_lo = st.enter_context(nc.sbuf_tensor("mlp_h_lo", [P, GC, T], F32R))
        acc = st.enter_context(nc.psum_tensor("mlp_acc", [P, 2, 1536], F32))
        fetched = [cx.sem(f"mlp_fetched{s}") for s in range(2)]
        hi_done, lo_done = cx.sem("mlp_hi_done"), cx.sem("mlp_lo_done")
        up_done, down_done = cx.sem("mlp_up_done"), cx.sem("mlp_down_done")
        relu_done, square_done, h_hi_done, h_lo_done = (cx.sem("mlp_relu_done"), cx.sem("mlp_square_done"),
                                                        cx.sem("mlp_h_hi_done"), cx.sem("mlp_h_lo_done"))
        added = cx.sem("mlp_added")
        OC = KC

        def as_up(w, s):
            return w[:, s, :].rearrange("p (k n) -> p k n", k=KC)

        def as_down(w, s):
            return w[:, s, :].rearrange("p (k n) -> p k n", k=GC)

        with nc.Block() as block:
            @block.sync
            def _(sp):
                def fetch(i, n):
                    s = n % 2
                    if n < 2:
                        col = i * G + n * (G // 2)
                        col = col if isinstance(i, int) else sp.snap(col)
                        src = w_up[:, ds(col, G // 2)].rearrange("(k p) n -> p k n", p=P)
                        dst = as_up(raw, s)
                    else:
                        row = i * G if isinstance(i, int) else sp.snap(i * G)
                        src = w_down[ds(row, G), (n - 2) * 512:(n - 1) * 512].rearrange("(k p) n -> p k n", p=P)
                        dst = as_down(raw, s)
                    sp.wait_ge(lo_done, i * 4 + n + 1)
                    sp.dma_start(dst, src).then_inc(fetched[s], 16)

                with sp.Fori(0, turns) as i:
                    for n in range(4):
                        fetch(i, n)

            @block.gpsimd
            def _(pool):
                pool.sem_inc(lo_done, 2)
                rows = WIN - TS
                with pool.Fori(0, turns) as i:
                    for n in range(4):
                        pool.wait_ge(hi_done, i * 4 + n + 1)
                        pool.tensor_tensor(out=w_lo[:, n % 2, :], in0=raw[:, n % 2, :],
                                           in1=w_hi[:, n % 2, :].bitcast(F32), op=ALU.subtract).then_inc(lo_done, 1)
                        src, dst = caches[n // 2]
                        r0 = (n % 2) * (rows // 2)
                        pool.dma_start(
                            dst[0, ds(i, 1), r0:r0 + rows // 2, :, :].rearrange("o (a r) h d -> (o a) (r h d)", a=15),
                            src[0, ds(i, 1), r0 + TS:r0 + TS + rows // 2, :, :].rearrange(
                                "o (a r) h d -> (o a) (r h d)", a=15)).then_inc(moved, 16)
                pool.wait_ge(moved, turns * 64)

            @block.scalar
            def _(act):
                def split_piece(i, n):
                    s = n % 2
                    act.wait_ge(fetched[s], i * 32 + (n // 2) * 16 + 16)
                    if n < 2:
                        act.wait_ge(down_done, i * OC + GC * (n + 1))
                    else:
                        act.wait_ge(up_done, i * GC + 2 * (n - 1))
                    act.activation(w_hi[:, s, :], raw[:, s, :], ACT.Copy).then_inc(hi_done, 1)

                def hidden(i, c):
                    s = c % 2
                    act.wait_ge(up_done, i * GC + c + 1)
                    act.wait_ge(h_lo_done, i * GC + c + 1)
                    act.activation(act_h[:, s, :], acc[:, s, 0:T], ACT.Relu).then_inc(relu_done, 1)
                    act.wait_ge(relu_done, i * GC + c + 3)
                    act.activation(act_h[:, s, :], act_h[:, s, :], ACT.Square).then_inc(square_done, 1)
                    if c == 0:
                        act.wait_ge(down_done, i * OC + OC)
                    act.wait_ge(square_done, i * GC + c + 1)
                    act.activation(h_hi[:, c, :], act_h[:, s, :], ACT.Copy).then_inc(h_hi_done, 1)

                with act.Fori(0, turns) as i:
                    split_piece(i, 0)
                    split_piece(i, 1)
                    hidden(i, 0)
                    hidden(i, 1)
                    split_piece(i, 2)
                    hidden(i, 2)
                    hidden(i, 3)
                    split_piece(i, 3)

            @block.tensor
            def _(pe):
                pe.sem_inc(down_done, OC)
                pe.sem_inc(relu_done, 2)
                with pe.Fori(0, turns) as i:
                    for c in range(GC):
                        if c % 2 == 0:
                            pe.wait_ge(lo_done, i * 4 + c // 2 + 3)
                        if c < 2:
                            pe.wait_ge(added, i * OC + OC - 1 + c)
                        else:
                            pe.wait_ge(relu_done, i * GC + c + 1)
                        s = c // 2
                        for k in range(KC):
                            last = split_products(pe, acc[:, c % 2, :], as_up(w_hi, s), as_up(w_lo, s), hi, lo, k, KC,
                                                  slice((c % 2) * P, (c % 2 + 1) * P))
                        last.then_inc(up_done, 1)
                    for c in range(OC):
                        if c % 4 == 0:
                            pe.wait_ge(lo_done, i * 4 + c // 4 + 5)
                        if c < 2:
                            pe.wait_ge(relu_done, i * GC + c + 5)
                        else:
                            pe.wait_ge(added, i * OC + OC + c - 1)
                        s = c // 4
                        for k in range(GC):
                            if c == 0:
                                pe.wait_ge(h_lo_done, i * GC + k + 3)
                            last = split_products(pe, acc[:, c % 2, :], as_down(w_hi, s), as_down(w_lo, s),
                                                  h_hi, h_lo, k, GC, slice((c % 4) * P, (c % 4 + 1) * P))
                        last.then_inc(down_done, 1)

            @block.vector
            def _(dve):
                dve.sem_inc(added, OC)
                dve.sem_inc(h_lo_done, 2)
                with dve.Fori(0, turns) as i:
                    for c in range(GC):
                        dve.wait_ge(h_hi_done, i * GC + c + 1)
                        dve.tensor_tensor(h_lo[:, c, :], act_h[:, c % 2, :], h_hi[:, c, :].bitcast(F32),
                                          ALU.subtract).then_inc(h_lo_done, 1)
                    for c in range(OC):
                        dve.wait_ge(down_done, i * OC + OC + c + 1)
                        dve.tensor_tensor(xT[:, c, :], xT[:, c, :], acc[:, c % 2, 0:T], ALU.add).then_inc(added, 1)


def store_tokens(nc, cx, yT, y_prompt, y_sample, ident):
    half = KC // 2
    with ExitStack() as st:
        y = st.enter_context(nc.sbuf_tensor("y", [P, 2, D_MODEL], F32))
        turned = st.enter_context(nc.psum_tensor("y_turned", [P, 2, D_MODEL], F32))
        turn_done, left_out, right_out, stored = (cx.sem("y_turn_done"), cx.sem("y_left_out"),
                                                  cx.sem("y_right_out"), cx.sem("y_stored"))
        tiles = [(t * P, P) for t in range(QT)] + [(SEQ, NS)]
        with nc.Block() as block:
            @block.tensor
            def _(pe):
                for t, (t0, n) in enumerate(tiles):
                    if t >= 2:
                        pe.wait_ge(left_out, t - 1)
                        pe.wait_ge(right_out, t - 1)
                    for c in range(KC):
                        last = pe.transpose(turned[0:n, t % 2, c * P:(c + 1) * P], yT[:, c, t0:t0 + n], ident[:, :])
                    last.then_inc(turn_done, 1)

            @block.vector
            def _(dve):
                for t, (t0, n) in enumerate(tiles):
                    dve.wait_ge(turn_done, t + 1)
                    if t >= 2:
                        dve.wait_ge(stored, 16 * (t - 1))
                    dve.tensor_copy(y[0:n, t % 2, 0:half * P], turned[0:n, t % 2, 0:half * P]).then_inc(left_out, 1)

            @block.scalar
            def _(act):
                for t, (t0, n) in enumerate(tiles):
                    act.wait_ge(turn_done, t + 1)
                    if t >= 2:
                        act.wait_ge(stored, 16 * (t - 1))
                    act.activation(y[0:n, t % 2, half * P:], turned[0:n, t % 2, half * P:], ACT.Copy).then_inc(right_out, 1)

            @block.sync
            def _(sp):
                for t, (t0, n) in enumerate(tiles):
                    sp.wait_ge(left_out, t + 1)
                    sp.wait_ge(right_out, t + 1)
                    dst = y_prompt[0, t0:t0 + n, :] if n == P else y_sample.rearrange("b t d -> (b t) d")
                    sp.dma_start(dst, y[0:n, t % 2, :]).then_inc(stored, 16)
                    sp.wait_ge(stored, 16 * (t + 1))


def bias_stage(nc, cx, rel_bias, one_hot, ln_count, by_distance):
    NB = rel_bias.shape[0]
    parts = [(a, min(512, LD - a)) for a in range(0, LD, 512)]
    with ExitStack() as st:
        rb = st.enter_context(nc.sbuf_tensor("bias_rb", [NB, HEADS], F32))
        oh = st.enter_context(nc.sbuf_tensor("bias_oh", [NB, LD], F32))
        lc = st.enter_context(nc.sbuf_tensor("bias_lc", [HEADS, LD], F32))
        fd = st.enter_context(nc.sbuf_tensor("bias_fd", [HEADS, LD], F32))
        acc = st.enter_context(nc.psum_tensor("bias_acc", [HEADS, len(parts), 512], F32))
        fetched, picked, summed, stored = (cx.sem("bias_fetched"), cx.sem("bias_picked"), cx.sem("bias_summed"),
                                           cx.sem("bias_stored"))
        with nc.Block() as block:
            @block.sync
            def _(sp):
                sp.dma_start(rb[:, :], rel_bias).then_inc(fetched, 16)
                sp.dma_start(oh[:, :], one_hot).then_inc(fetched, 16)
                sp.dma_start(lc[:, :], ln_count).then_inc(fetched, 16)
                sp.wait_ge(summed, len(parts))
                sp.dma_start(by_distance, fd[:, :]).then_inc(stored, 16)
                sp.wait_ge(stored, 16)

            @block.tensor
            def _(pe):
                pe.wait_ge(fetched, 48)
                for j, (a, n) in enumerate(parts):
                    pe.matmul(acc[:, j, 0:n], rb[:, :], oh[:, a:a + n], start=True, stop=True).then_inc(picked, 1)

            @block.vector
            def _(dve):
                dve.wait_ge(fetched, 48)
                for j, (a, n) in enumerate(parts):
                    dve.wait_ge(picked, j + 1)
                    dve.tensor_tensor(fd[:, a:a + n], lc[:, a:a + n], acc[:, j, 0:n], ALU.add).then_inc(summed, 1)


def prompt_stage(nc, cx, qkvT, oT, by_distance, sb_bias, neg_causal, ident, outs):
    SB, DIL = 0, 1
    NU = 4 * QT
    GRP = 9
    units = [(u // (2 * QT), (u % (2 * QT)) // 2, u % 2) for u in range(NU)]
    with ExitStack() as st:
        def sb(name, shape, dt=F32):
            return st.enter_context(nc.sbuf_tensor(f"pr_{name}", shape, dt))

        qkv = sb("qkv", [P, 6, T])
        nat = sb("nat", [P, 4, QT, P])
        natS = sb("natS", [NS, 4, P])
        q_back = sb("q_back", [P, QT, P])
        bias = sb("bias", [P, HEADS, SEQ])
        stay = sb("stay", [P, 2, SEQ])
        take = sb("take", [P, 2, SEQ])
        prod = sb("prod", [P, SEQ + 1])
        wts = sb("wts", [P, 2, SEQ])
        wtsT = sb("wtsT", [P, 2, SEQ])
        o_nat = sb("o_nat", [P, 2, QT, P])
        o_T = sb("o_T", [P, 2, SEQ])
        top = sb("top", [P, 2, 2])
        den = sb("den", [P, 2 * QT])
        inv = sb("inv", [P, 2 * QT])
        zb = sb("zb", [P, 2, HEADS])
        maskb = sb("maskb", [P, P], BF16)
        identb = sb("identb", [P, P], BF16)
        s_ps = st.enter_context(nc.psum_tensor("pr_scores", [P, 4, 512], F32))
        t_ps = st.enter_context(nc.psum_tensor("pr_turned", [P, SEQ], F32))
        o_ps = st.enter_context(nc.psum_tensor("pr_o", [P, 2, 512], F32))

        ready = {n: cx.sem(f"pr_{n}") for n in (
            "tables_in", "tables_ready", "in", "in_free", "nat_turned", "nat_out_v", "nat_out_a", "nat_stored", "nat_free", "oT_free", "scored",
            "sb_gates", "sb_scanned", "sb_weights", "logits", "topped", "lowered", "dil_weights", "turned", "turned_out",
            "o_done", "inverted", "o_out", "o_turned", "oT_out_v", "oT_out_a", "oT_stored")}
        tables_in, tables_ready, loaded, in_free = (ready[n] for n in ("tables_in", "tables_ready", "in", "in_free"))
        nat_turned, nat_out_v, nat_out_a, nat_stored = (ready[n] for n in ("nat_turned", "nat_out_v", "nat_out_a",
                                                                          "nat_stored"))
        scored, sb_gates, sb_scanned, sb_weights = (ready[n] for n in ("scored", "sb_gates", "sb_scanned",
                                                                      "sb_weights"))
        logits, topped, lowered, dil_weights = (ready[n] for n in ("logits", "topped", "lowered", "dil_weights"))
        turned, turned_out, o_done, inverted, o_out = (ready[n] for n in ("turned", "turned_out", "o_done",
                                                                         "inverted", "o_out"))
        q_turned_back = cx.sem("pr_q_turned_back")
        nat_free, oT_free = ready["nat_free"], ready["oT_free"]
        o_turned, oT_out_v, oT_out_a, oT_stored = (ready[n] for n in ("o_turned", "oT_out_v", "oT_out_a", "oT_stored"))

        def forwards(g):
            a = (g % 2) * 512
            dst = o_T[:, g // 2, a:a + 512].rearrange("p (q i) -> p q i", i=P)
            src = s_ps[:, g, :].rearrange("p (q i) -> p q i", i=P)
            return dst, src[:, :, ::-1] if g // 2 == DIL else src

        def width(t):
            return (units[t][1] + 1) * P

        def scores_of(t):
            return s_ps[:, 2 * (t % 2):2 * (t % 2) + 2, :].rearrange("p b n -> p (b n)")[:, 0:width(t)]

        def scores_free(eng, j, t):
            kind, r = units[t][0], t % (2 * QT)
            eng.wait_ge(sb_gates if kind == SB else logits, j * 2 * QT + r + 1)

        def weighed(eng, j, t):
            kind, r = units[t][0], t % (2 * QT)
            eng.wait_ge(sb_weights if kind == SB else dil_weights, j * 2 * QT + r + 1)

        with nc.Block() as block:
            @block.sync
            def _(sp):
                sp.dma_start(zb[:, 0, :], bass.AP(
                    sb_bias.tensor, sb_bias.offset, [[0, P], [1, HEADS]])).then_inc(tables_in, 16)
                for h in range(HEADS):
                    first = by_distance.offset + h * LD + DIST0 - (SEQ - 1)
                    sp.dma_start(bias[:, h, :], bass.AP(by_distance.tensor, first, [[1, P], [1, SEQ]])).then_inc(tables_in, 16)
                with sp.Fori(0, PAIRS) as j:
                    rows = [sp.snap(j * P + g * W) for g in range(6)]
                    sp.wait_ge(in_free, j + 1)
                    for g in range(6):
                        sp.dma_start(qkv[:, g, :], qkvT[ds(rows[g], P), :]).then_inc(loaded, 16)

            @block.gpsimd
            def _(pool):
                pool.sem_inc(nat_free, 1)
                pool.sem_inc(oT_free, 1)
                with pool.Fori(0, PAIRS) as j:
                    pool.wait_ge(nat_out_v, j * 5 + 5)
                    pool.wait_ge(nat_out_a, j * 4 + 4)
                    for w in range(4):
                        prompt, sample = outs[w]
                        pool.dma_start(prompt[0, 0].rearrange("(t p) h d -> p t (h d)", p=P)[:, :, ds(j * P, P)],
                                       nat[:, w, :, :]).then_inc(nat_stored, 16)
                        pool.dma_start(sample.rearrange("b t h d -> b t (h d)")[:, :, ds(j * P, P)],
                                       natS[:, w, :]).then_inc(nat_stored, 16)
                    pool.wait_ge(oT_out_v, j * 2 + 2)
                    pool.wait_ge(oT_out_a, j * 2 + 2)
                    for kind in (SB, DIL):
                        pool.dma_start(oT[ds(j * P + kind * W, P), 0:SEQ], o_T[:, kind, :]).then_inc(oT_stored, 16)
                    pool.wait_ge(nat_stored, j * 128 + 128)
                    pool.sem_inc(nat_free, 1)
                    pool.wait_ge(oT_stored, j * 32 + 32)
                    pool.sem_inc(oT_free, 1)

            @block.tensor
            def _(pe):
                pe.sem_inc(in_free, 1)
                pe.wait_ge(tables_ready, 3)

                def nat_group_out(j, g):
                    if g % 2 == 0:
                        pe.wait_ge(nat_out_v, j * 5 + g // 2 + 1)
                    else:
                        pe.wait_ge(nat_out_a, j * 4 + g // 2 + 1)

                def score(j, t):
                    kind, q, h = units[t]
                    if t >= 2:
                        scores_free(pe, j, t - 2)
                    if t == 2 * QT:
                        pe.wait_ge(q_turned_back, j + 1)
                    n, rows = width(t), slice(h * HD, (h + 1) * HD)
                    out = scores_of(t)
                    for a in range(0, n, 512):
                        b = min(n, a + 512)
                        qs = qkv[rows, 0, q * P:(q + 1) * P] if kind == SB else q_back[rows, q, :]
                        last = pe.matmul(out[:, a:b], qs,
                                         qkv[rows, 3 * kind + 1, a:b], start=True, stop=(kind == DIL or b < n))
                    if kind == SB:
                        last = pe.matmul(out[:, n - P:n], identb[:, :], maskb[:, :], start=False, stop=True)
                    last.then_inc(scored, 1)

                def turn(j, t):
                    weighed(pe, j, t)
                    if t >= 1:
                        pe.wait_ge(turned_out, j * NU + t)
                    for a in range(0, width(t), P):
                        last = pe.transpose(t_ps[:, a:a + P], wts[:, t % 2, a:a + P], ident[:, :])
                    last.then_inc(turned, 1)

                def values(j, t):
                    kind, q, h = units[t]
                    pe.wait_ge(turned_out, j * NU + t + 1)
                    if t >= 2:
                        pe.wait_ge(o_out, j * NU + t - 1)
                    for c in range(q + 1):
                        last = pe.matmul(o_ps[:, t % 2, 0:HD], wtsT[:, t % 2, c * P:(c + 1) * P],
                                         nat[:, 2 * kind + 1, c, h * HD:(h + 1) * HD], start=(c == 0), stop=(c == q))
                    last.then_inc(o_done, 1)

                with pe.Fori(0, PAIRS) as j:
                    pe.wait_ge(loaded, j * 96 + 96)
                    for g in range(GRP):
                        if g >= 4:
                            nat_group_out(j, g - 4)
                            pe.sem_inc(cx.passed, 1)
                        for i in range(4):
                            if g < 8:
                                w, c = g // 2, (g % 2) * 4 + i
                                src = qkv[:, 3 * (w // 2) + 1 + w % 2, c * P:(c + 1) * P]
                                last = pe.transpose(s_ps[:, g % 4, i * P:(i + 1) * P], src, ident[:, :])
                            else:
                                src = qkv[:, 3 * (i // 2) + 1 + i % 2, SEQ:T]
                                last = pe.transpose(s_ps[0:NS, 0, i * P:(i + 1) * P], src, ident[:, :])
                        last.then_inc(nat_turned, 1)
                    for g in range(5, GRP):
                        nat_group_out(j, g)
                    score(j, 0)
                    score(j, 1)
                    for t in range(NU):
                        if t + 2 < NU:
                            score(j, t + 2)
                        turn(j, t)
                        if t >= 1:
                            values(j, t - 1)
                    values(j, NU - 1)
                    pe.wait_ge(o_out, j * NU + NU)
                    pe.sem_inc(in_free, 1)
                    for g in range(4):
                        for i in range(4):
                            last = pe.transpose(s_ps[:, g, i * P:(i + 1) * P], o_nat[:, g // 2, (g % 2) * 4 + i, :],
                                                ident[:, :])
                        last.then_inc(o_turned, 1)
                    pe.wait_ge(oT_out_v, j * 2 + 2)
                    pe.wait_ge(oT_out_a, j * 2 + 2)

            @block.scalar
            def _(act):
                def turned_away(j, t):
                    act.wait_ge(turned, j * NU + t + 1)
                    if t >= 2:
                        act.wait_ge(o_done, j * NU + t - 1)
                    act.activation(wtsT[:, t % 2, 0:width(t)], t_ps[:, 0:width(t)], ACT.Copy).then_inc(turned_out, 1)

                act.wait_ge(tables_ready, 4)
                with act.Fori(0, PAIRS) as j:
                    for g in range(1, GRP, 2):
                        act.wait_ge(nat_turned, j * GRP + g + 1)
                        if g == 1:
                            act.wait_ge(nat_free, j + 1)
                        act.activation(nat[:, g // 2, 4 * (g % 2):4 * (g % 2) + 4, :].rearrange("p c n -> p (c n)"),
                                       s_ps[:, g % 4, :], ACT.Copy).then_inc(nat_out_a, 1)
                    for t in range(NU):
                        kind, q, h = units[t]
                        n, r, s = width(t), t % (2 * QT), t % 2
                        if kind == SB:
                            act.wait_ge(scored, j * NU + t + 1)
                            if t >= 2:
                                act.wait_ge(sb_weights, j * 2 * QT + r - 1)
                            act.sem_inc(cx.passed, 1)
                            act.activation(take[:, s, 0:n], scores_of(t), ACT.Sigmoid, scale=SCALE,
                                           bias=zb[:, 0, ds(j * 2 + h, 1)])
                            act.activation(stay[:, s, 0:n], scores_of(t), ACT.Sigmoid, scale=-SCALE,
                                           bias=zb[:, 1, ds(j * 2 + h, 1)]).then_inc(sb_gates, 1)
                        else:
                            act.wait_ge(lowered, j * 2 * QT + r + 1)
                            act.wait_ge(turned, j * NU + t - 1)
                            act.activation(wts[:, s, 0:n], take[:, s, 0:n], ACT.Exp, bias=top[:, s, 1:2],
                                           accum_out=den[:, r:r + 1]).then_inc(dil_weights, 1)
                        if t >= 1:
                            turned_away(j, t - 1)
                    turned_away(j, NU - 1)
                    for g in (1, 3):
                        act.wait_ge(o_turned, j * 4 + g + 1)
                        if g == 1:
                            act.wait_ge(oT_free, j + 1)
                        act.activation(*forwards(g), ACT.Copy).then_inc(oT_out_a, 1)

            @block.vector
            def _(dve):
                dve.memset(prod[:, SEQ:SEQ + 1], 1.0).then_inc(tables_ready, 1)
                dve.tensor_copy(maskb[:, :], neg_causal[:, :]).then_inc(tables_ready, 1)
                dve.tensor_copy(identb[:, :], ident[:, :]).then_inc(tables_ready, 1)
                dve.wait_ge(tables_in, 16 * (HEADS + 1))
                dve.tensor_scalar(zb[:, 1, :], zb[:, 0, :], -1.0, None, ALU.mult).then_inc(tables_ready, 1)
                dve.wait_ge(tables_ready, 4)

                def out_of_psum(j, t):
                    kind, q, h = units[t]
                    dve.wait_ge(o_done, j * NU + t + 1)
                    dst, src = o_nat[:, kind, q, h * HD:(h + 1) * HD], o_ps[:, t % 2, 0:HD]
                    if kind == SB:
                        dve.tensor_copy(dst, src).then_inc(o_out, 1)
                    else:
                        r = t % (2 * QT)
                        dve.reciprocal(inv[:, r:r + 1], den[:, r:r + 1]).then_inc(inverted, 1)
                        dve.wait_ge(inverted, j * 2 * QT + r + 1)
                        dve.tensor_scalar(dst, src, inv[:, r:r + 1], None, ALU.mult).then_inc(o_out, 1)

                with dve.Fori(0, PAIRS) as j:
                    dve.wait_ge(loaded, j * 96 + 96)
                    dve.tensor_copy(q_back[:, :, :], qkv[:, 3, 0:SEQ].rearrange("p (q i) -> p q i", i=P)[:, :, ::-1])\
                       .then_inc(q_turned_back, 1)
                    for g in range(0, GRP, 2):
                        dve.wait_ge(nat_turned, j * GRP + g + 1)
                        if g == 0:
                            dve.wait_ge(nat_free, j + 1)
                        if g < 8:
                            dve.tensor_copy(nat[:, g // 2, 0:4, :].rearrange("p c n -> p (c n)"),
                                            s_ps[:, g % 4, :]).then_inc(nat_out_v, 1)
                        else:
                            dve.tensor_copy(natS[:, :, :].rearrange("p c n -> p (c n)"),
                                            s_ps[0:NS, 0, :]).then_inc(nat_out_v, 1)
                    for t in range(NU):
                        kind, q, h = units[t]
                        n, r, s = width(t), t % (2 * QT), t % 2
                        if kind == SB:
                            dve.wait_ge(sb_gates, j * 2 * QT + r + 1)
                            if t >= 1:
                                dve.wait_ge(sb_weights, j * 2 * QT + r)
                            back = stay[:, s, 0:n][:, ::-1]
                            dve.tensor_tensor_scan(prod[:, SEQ - n:SEQ][:, ::-1], back, back, 1.0, ALU.mult,
                                                   ALU.bypass).then_inc(sb_scanned, 1)
                            dve.wait_ge(sb_scanned, j * 2 * QT + r + 1)
                            if t >= 2:
                                dve.wait_ge(turned, j * NU + t - 1)
                            dve.tensor_tensor(wts[:, s, 0:n], take[:, s, 0:n], prod[:, SEQ + 1 - n:SEQ + 1],
                                              ALU.mult).then_inc(sb_weights, 1)
                        else:
                            dve.wait_ge(scored, j * NU + t + 1)
                            if r >= 2:
                                dve.wait_ge(dil_weights, j * 2 * QT + r - 1)
                            else:
                                dve.wait_ge(sb_weights, j * 2 * QT + 2 * QT)
                            head_bias = bias[:, ds(j * 2 + h, 1), SEQ - n:SEQ].rearrange("p o n -> p (o n)")
                            dve.scalar_tensor_tensor(out=take[:, s, 0:n], in0=scores_of(t), scalar=SCALE,
                                                     in1=head_bias, op0=ALU.mult, op1=ALU.add).then_inc(logits, 1)
                            dve.wait_ge(logits, j * 2 * QT + r + 1)
                            dve.tensor_reduce(top[:, s, 0:1], take[:, s, 0:n], AX_X, ALU.max).then_inc(topped, 1)
                            dve.wait_ge(topped, j * 2 * QT + r + 1)
                            dve.tensor_scalar(top[:, s, 1:2], top[:, s, 0:1], -1.0, None, ALU.mult).then_inc(lowered, 1)
                        if t >= 2:
                            out_of_psum(j, t - 2)
                    out_of_psum(j, NU - 2)
                    out_of_psum(j, NU - 1)
                    for g in (0, 2):
                        dve.wait_ge(o_turned, j * 4 + g + 1)
                        if g == 0:
                            dve.wait_ge(oT_free, j + 1)
                        dve.tensor_copy(*forwards(g)).then_inc(oT_out_v, 1)


def sample_stage(nc, cx, qkvT, oT, by_distance, sb_bias, page_table, sb_caches, win_caches, new_v, neg_new, own_head,
                 same_token, ident):
    DIL, SB = 0, 1
    R = NS
    NU, LAG = 12, 3
    tiles = [4, 4, 2, 0] + [4] * 8
    new = [False, False, True, True] + [False] * 8
    kind = [DIL] * 3 + [SB] * 9
    wide = [n * P + (TS if x else 0) for n, x in zip(tiles, new)]
    offs = [0, 512, 1024]
    NL = sum(wide[0:3])
    KS, VS = 4, 6
    k_before = [sum(tiles[m] for m in range(n) if m % KS == n % KS) for n in range(NU + KS)][0:NU]
    v_size = [t + x for t, x in zip(tiles, new)]
    v_before = [sum(v_size[m] for m in range(n) if m % VS == n % VS) for n in range(NU)]
    k_turn = [sum(tiles[s::KS]) for s in range(KS)]
    v_turn = [sum(v_size[s::VS]) for s in range(VS)]
    has = [n for n in range(NU) if tiles[n]]
    t_count = [sum(m <= n for m in has) for n in range(NU)]
    NT = len(has)
    use = {n: n + (n > 3) for n in range(NU)}
    use_o = {DIL: 4, SB: 13}
    NUSE = 14
    with ExitStack() as st:
        def sb(name, shape, dt=F32):
            return st.enter_context(nc.sbuf_tensor(f"sa_{name}", shape, dt))

        k_in = sb("k_in", [P, KS, 4, W])
        v_in = sb("v_in", [P, VS, 4, W])
        kT = sb("kT", [P, 2, PAIRS, 512])
        new_qk = sb("new_qk", [P, 4, PAIRS, NS])
        newk = sb("newk", [P, 2, PAIRS, TS])
        qd = sb("qd", [P, 2, PAIRS * (NS + 2)])
        bias = sb("bias", [R, WIN + TS])
        logit = sb("logit", [R, NL])
        expd = sb("expd", [R, NL])
        take = sb("take", [R, 2, 512])
        stay = sb("stay", [R, 2, 512])
        prod = sb("prod", [R, 2, 513])
        wts = sb("wts", [R, 4, 512])
        wtsT = sb("wtsT", [P, 2, 5 * R])
        own = sb("own", [R, W])
        o_own = sb("o_own", [R, 2, W])
        tok = sb("tok", [R, TS])
        o_all = sb("o_all", [P, 2, PAIRS, NS])
        zb = sb("zb", [R, 2])
        top = sb("top", [R, 4])
        maskf = sb("maskf", [R, TS])
        maskb = sb("maskb", [R, TS], BF16)
        identb = sb("identb", [R, R], BF16)
        pages = sb("pages", [1, B * PAGES], I32)
        kt_ps = st.enter_context(nc.psum_tensor("sa_kt", [P, PAIRS, 512], F32))
        s_ps = st.enter_context(nc.psum_tensor("sa_s", [R, 2, 512], F32))
        w_ps = st.enter_context(nc.psum_tensor("sa_w", [P, 512], F32))
        o_ps = st.enter_context(nc.psum_tensor("sa_o", [R, 512], F32))

        tables_in, tables_ready = cx.sem("sa_tables_in"), cx.sem("sa_tables_ready")
        pages_in = cx.sem("sa_pages_in")
        k_loaded = [cx.sem(f"sa_k_loaded{s}") for s in range(KS)]
        v_loaded = [cx.sem(f"sa_v_loaded{s}") for s in range(VS)]
        q_ready, k_turned, kT_out_a, kT_out_v = (cx.sem("sa_q_ready"), cx.sem("sa_k_turned"), cx.sem("sa_kT_out_a"),
                                                 cx.sem("sa_kT_out_v"))
        scored, gates, carried, scanned, sb_weights = (cx.sem("sa_scored"), cx.sem("sa_gates"), cx.sem("sa_carried"),
                                                       cx.sem("sa_scanned"), cx.sem("sa_sb_weights"))
        logits, topped, lowered, dil_weights = (cx.sem("sa_logits"), cx.sem("sa_topped"), cx.sem("sa_lowered"),
                                                cx.sem("sa_dil_weights"))
        w_turned, w_out, valued, inverted, owned, stored = (cx.sem("sa_w_turned"), cx.sem("sa_w_out"),
                                                            cx.sem("sa_valued"), cx.sem("sa_inverted"),
                                                            cx.sem("sa_owned"), cx.sem("sa_stored"))

        def qd_of(k, pair):
            return qd[:, k, pair * NS:(pair + 1) * NS]

        with nc.Block() as block:
            @block.sync
            def _(sp):
                sp.dma_start(pages[:, :], page_table.rearrange("b n -> (b n)").rearrange("(o n) -> o n", o=1)).then_inc(pages_in, 16)
                n_tables = 0
                for g, row in enumerate((3 * W, 4 * W, 0, W)):
                    sp.dma_start(new_qk[:, g, :, :], qkvT[row:row + W, SEQ:T].rearrange(
                        "(c p) t -> p c t", p=P)).then_inc(tables_in, 16)
                for t in range(TS):
                    rows = slice(t * HEADS, (t + 1) * HEADS)
                    sp.dma_start(bias[rows, :], by_distance[:, TS - 1 - t:TS - 1 - t + WIN + TS]).then_inc(tables_in, 16)
                    sp.dma_start(zb[rows, 0:1], sb_bias[0:1, :].rearrange("o h -> h o"),
                                 allow_slow_non_contiguous=True).then_inc(tables_in, 16)
                sp.dma_start(own[:, :], own_head).then_inc(tables_in, 16)
                sp.dma_start(tok[:, :], same_token).then_inc(tables_in, 16)
                sp.dma_start(maskf[:, :], neg_new).then_inc(tables_in, 16)
                sp.wait_ge(pages_in, 16)

                def window_tile(cache, b, c):
                    if c < 6:
                        return cache[0, ds(b, 1), c * 256:(c + 1) * 256, :, :].rearrange(
                            "o (a r) h d -> (o a) r (h d)", r=16)[:, 0:TS, :]
                    return cache[0, ds(b, 1), 1536 + (c - 6) * P:1536 + (c - 5) * P, :, :].rearrange(
                        "o r h d -> (o r) (h d)")

                def load(b, n, ring, slot, sem, cache_w, cache_p):
                    sp.sem_inc(cx.passed, 1)
                    for i in range(tiles[n]):
                        if kind[n] == DIL:
                            sp.dma_start(ring[:, slot, i, :], window_tile(cache_w, b, 4 * n + i)).then_inc(sem, 16)
                        else:
                            page = sp.value_load(pages[0:1, ds(b * PAGES + (4 * (NU - 1 - n) + i), 1)],
                                                 min_val=0, max_val=sb_caches[0].shape[1] - 1)
                            sp.dma_start(ring[:, slot, i, :], cache_p[0, ds(page, 1), :, :, :].rearrange(
                                "o r h d -> (o r) (h d)")).then_inc(sem, 16)

                def load_keys(b, n):
                    if tiles[n]:
                        before = NT + t_count[n - KS] if n >= KS else t_count[n - KS + NU]
                        sp.wait_ge(k_turned, b * NT + before)
                        load(b, n, k_in, n % KS, k_loaded[n % KS], win_caches[0], sb_caches[0])

                def load_values(b, n):
                    sp.wait_ge(valued, b * NU + (NU + n - VS + 1 if n >= VS else n - VS + NU + 1))
                    s = n % VS
                    load(b, n, v_in, s, v_loaded[s], win_caches[1], sb_caches[1])
                    if new[n]:
                        sp.dma_start(v_in[0:TS, s, tiles[n], :], new_v[kind[n]][ds(b, 1)].rearrange(
                            "o t h d -> (o t) (h d)")).then_inc(v_loaded[s], 16)

                with sp.Fori(0, B) as b:
                    for n in range(NU):
                        load_keys(b, n)
                        if n >= 2:
                            load_values(b, n - 2)
                    load_values(b, NU - 2)
                    load_values(b, NU - 1)
                for k in (DIL, SB):
                    sp.wait_ge(w_out, B * NUSE + 1)
                    row = 0 if k == SB else W
                    sp.dma_start(oT[row:row + W, SEQ:T].rearrange("(c p) t -> p c t", p=P), o_all[:, k, :, :])\
                      .then_inc(stored, 16)
                sp.wait_ge(stored, 32)

            @block.tensor
            def _(pe):
                pe.sem_inc(k_turned, NT)
                pe.sem_inc(valued, NU)
                pe.wait_ge(tables_ready, 4)

                def turn_keys(b, n):
                    if not tiles[n]:
                        return
                    s = n % KS
                    pe.wait_ge(k_loaded[s], b * (16 * k_turn[s]) + 16 * (k_before[n] + tiles[n]))
                    for c in range(PAIRS):
                        for i in range(tiles[n]):
                            last = pe.transpose(kt_ps[:, c, i * P:(i + 1) * P], k_in[:, s, i, c * P:(c + 1) * P], ident[:, :])
                    last.then_inc(k_turned, 1)

                def score(b, n):
                    if tiles[n]:
                        pe.wait_ge(kT_out_a, b * NT + t_count[n])
                        pe.wait_ge(kT_out_v, b * NT + t_count[n])
                    if n >= 2:
                        m = n - 2
                        if kind[m] == DIL:
                            pe.wait_ge(logits, b * 3 + m + 1)
                        else:
                            pe.wait_ge(gates, b * 9 + m - 2)
                    k, w = kind[n], tiles[n] * P
                    if w:
                        for c in range(PAIRS):
                            last = pe.matmul(s_ps[:, n % 2, 0:w], qd_of(k, c), kT[:, n % 2, c, 0:w],
                                             start=(c == 0), stop=(c == PAIRS - 1))
                    if new[n]:
                        for c in range(PAIRS):
                            last = pe.matmul(s_ps[:, n % 2, w:w + TS], qd_of(k, c), newk[:, k, c, :],
                                             start=(c == 0), stop=(c == PAIRS - 1 and k == DIL))
                        if k == SB:
                            last = pe.matmul(s_ps[:, n % 2, w:w + TS], identb[:, :], maskb[:, :], start=False, stop=True)
                    last.then_inc(scored, 1)

                def bank_free(b, u):
                    pe.wait_ge(w_out, b * NUSE + u + 1)

                def turn_weights(b, n):
                    if kind[n] == DIL:
                        pe.wait_ge(dil_weights, b + 1)
                        src = expd[:, offs[n]:offs[n] + wide[n]]
                    else:
                        pe.wait_ge(sb_weights, b * 9 + n - 2)
                        src = wts[:, n % 4, 0:wide[n]]
                    bank_free(b, use[n])
                    pe.sem_inc(cx.passed, 1)
                    for i in range(tiles[n]):
                        last = pe.transpose(w_ps[:, i * R:(i + 1) * R], src[:, i * P:(i + 1) * P], ident[0:R, 0:R])
                    if new[n]:
                        i = tiles[n]
                        last = pe.transpose(w_ps[0:TS, i * R:(i + 1) * R], src[:, i * P:i * P + TS], ident[0:R, 0:R])
                    last.then_inc(w_turned, 1)

                def values(b, n):
                    s = n % VS
                    pe.wait_ge(w_out, b * NUSE + use[n] + 2)
                    pe.wait_ge(v_loaded[s], b * (16 * v_turn[s]) + 16 * (v_before[n] + v_size[n]))
                    ends = n in (2, NU - 1)
                    for i in range(v_size[n]):
                        rows = P if i < tiles[n] else TS
                        last = pe.matmul(o_ps[:, :], wtsT[0:rows, n % 2, i * R:(i + 1) * R], v_in[0:rows, s, i, :],
                                         start=(n in (0, 3) and i == 0), stop=(ends and i == v_size[n] - 1))
                    last.then_inc(valued, 1)

                def place(b, k):
                    pe.wait_ge(owned, b * 2 + k + 1)
                    bank_free(b, use_o[k])
                    for c in range(PAIRS):
                        last = pe.matmul(w_ps[:, c * TS:(c + 1) * TS], o_own[:, k, c * P:(c + 1) * P], tok[:, :],
                                         start=True, stop=True)
                    last.then_inc(w_turned, 1)

                with pe.Fori(0, B) as b:
                    turn_keys(b, 0)
                    pe.wait_ge(q_ready, b + 1)
                    for s in range(NU + LAG + 1):
                        if s < NU:
                            score(b, s)
                        if s + 1 < NU:
                            turn_keys(b, s + 1)
                        if s == 7:
                            place(b, DIL)
                        if 0 <= s - LAG < NU:
                            turn_weights(b, s - LAG)
                        if 0 <= s - LAG - 1 < NU:
                            values(b, s - LAG - 1)
                    place(b, SB)

            def keys_out(eng, out, b, n, copy, sem, c0):
                if not tiles[n]:
                    return
                eng.wait_ge(k_turned, b * NT + NT + t_count[n])
                if n >= 2:
                    eng.wait_ge(scored, b * NU + n - 1)
                w = tiles[n] * P
                copy(out[:, n % 2, c0:c0 + 2, 0:w], kt_ps[:, c0:c0 + 2, 0:w]).then_inc(sem, 1)

            @block.scalar
            def _(act):
                act.wait_ge(tables_ready, 5)

                def copy(out, x):
                    return act.activation(out, x, ACT.Copy)

                def weights_out(b, n):
                    act.wait_ge(w_turned, b * NUSE + use[n] + 1)
                    if n >= 2:
                        act.wait_ge(valued, b * NU + NU + n - 1)
                    w = tiles[n] * R
                    if w:
                        last = copy(wtsT[:, n % 2, 0:w], w_ps[:, 0:w])
                        if not new[n]:
                            last.then_inc(w_out, 1)
                    if new[n]:
                        copy(wtsT[0:TS, n % 2, w:w + R], w_ps[0:TS, w:w + R]).then_inc(w_out, 1)

                def placed(b, k):
                    act.wait_ge(w_turned, b * NUSE + use_o[k] + 1)
                    act.sem_inc(cx.passed, 1)
                    copy(o_all[:, k, :, ds(b * TS, TS)], w_ps[:, 0:PAIRS * TS].rearrange("p (c t) -> p c t", t=TS))\
                        .then_inc(w_out, 1)

                with act.Fori(0, B) as b:
                    keys_out(act, kT, b, 0, copy, kT_out_a, 0)
                    for s in range(NU + LAG + 1):
                        if s == 3:
                            act.wait_ge(lowered, b + 1)
                            act.activation(expd[:, :], logit[:, :], ACT.Exp, bias=top[:, 1:2],
                                           accum_out=top[:, 2:3]).then_inc(dil_weights, 1)
                        if s + 1 < NU:
                            keys_out(act, kT, b, s + 1, copy, kT_out_a, 0)
                        if s < NU and kind[s] == SB:
                            act.wait_ge(scored, b * NU + s + 1)
                            if s >= 5:
                                act.wait_ge(sb_weights, b * 9 + s - 4)
                            w = wide[s]
                            act.activation(take[:, s % 2, 0:w], s_ps[:, s % 2, 0:w], ACT.Sigmoid, scale=SCALE, bias=zb[:, 0:1])
                            act.activation(stay[:, s % 2, 0:w], s_ps[:, s % 2, 0:w], ACT.Sigmoid, scale=-SCALE,
                                           bias=zb[:, 1:2]).then_inc(gates, 1)
                        if s == 7:
                            placed(b, DIL)
                        if 0 <= s - LAG < NU:
                            weights_out(b, s - LAG)
                    placed(b, SB)

            @block.vector
            def _(dve):
                dve.sem_inc(w_out, 1)
                dve.memset(qd[:, :, :], 0.0).then_inc(tables_ready, 1)
                dve.wait_ge(tables_in, 16 * (4 + 2 * TS + 3))
                dve.tensor_copy(maskb[:, :], maskf[:, :]).then_inc(tables_ready, 1)
                dve.tensor_copy(identb[:, :], ident[0:R, 0:R]).then_inc(tables_ready, 1)
                dve.memset(prod[:, :, 512:513], 1.0).then_inc(tables_ready, 1)
                dve.tensor_scalar(zb[:, 1:2], zb[:, 0:1], -1.0, None, ALU.mult).then_inc(tables_ready, 1)
                dve.wait_ge(tables_ready, 5)

                def copy(out, x):
                    return dve.tensor_copy(out, x)

                def queries(b):
                    for k in (DIL, SB):
                        dve.tensor_copy(newk[:, k, :, :], new_qk[:, 2 * k + 1, :, ds(b * TS, TS)])
                        for half in range(2):
                            rows = slice(half * HD, (half + 1) * HD)
                            dst = qd[rows, k, :].rearrange("p (c x) -> p c x", x=NS + 2)[:, :, half:half + NS - 7:HEADS]
                            last = dve.tensor_copy(dst, new_qk[rows, 2 * k, :, ds(b * TS, TS)])
                    last.then_inc(q_ready, 1)

                def dilated(b, n):
                    dve.wait_ge(scored, b * NU + n + 1)
                    w, o = wide[n], offs[n]
                    spans = []
                    sparse = max(0, min(tiles[n], 6 - 4 * n)) * P
                    if sparse:
                        g = bias[:, 0:1536].rearrange("p (a r) -> p a r", r=16)[:, :, 0:TS]
                        spans.append((0, sparse, g[:, o // TS:(o + sparse) // TS, :]))
                    if sparse < w:
                        pos = 1536 + o + sparse - 768
                        spans.append((sparse, w, bias[:, pos:pos + w - sparse]))
                    for a, e, g in spans:
                        x, y = s_ps[:, n % 2, a:e], logit[:, o + a:o + e]
                        if len(g.shape) == 3:
                            x, y = (z.rearrange("p (a r) -> p a r", r=TS) for z in (x, y))
                        last = dve.scalar_tensor_tensor(out=y, in0=x, scalar=SCALE, in1=g, op0=ALU.mult, op1=ALU.add)
                    last.then_inc(logits, 1)
                    if n == 2:
                        dve.wait_ge(logits, b * 3 + 3)
                        dve.tensor_reduce(top[:, 0:1], logit[:, :], AX_X, ALU.max).then_inc(topped, 1)
                        dve.wait_ge(topped, b + 1)
                        dve.tensor_scalar(top[:, 1:2], top[:, 0:1], -1.0, None, ALU.mult).then_inc(lowered, 1)

                def broken(b, n):
                    w, s = wide[n], n % 2
                    if n == 3:
                        dve.memset(prod[:, s, 512:513], 1.0).then_inc(carried, 1)
                    else:
                        dve.tensor_copy(prod[:, s, 512:513], prod[:, 1 - s, 512 - wide[n - 1]:513 - wide[n - 1]])\
                           .then_inc(carried, 1)
                    dve.wait_ge(carried, b * 9 + n - 2)
                    dve.wait_ge(gates, b * 9 + n - 2)
                    back = stay[:, s, 0:w][:, ::-1]
                    dve.tensor_tensor_scan(prod[:, s, 512 - w:512][:, ::-1], back, back, prod[:, s, 512:513],
                                           ALU.mult, ALU.bypass).then_inc(scanned, 1)
                    dve.wait_ge(scanned, b * 9 + n - 2)
                    if n >= 7:
                        dve.wait_ge(w_turned, b * NUSE + use[n - 4] + 1)
                    dve.tensor_tensor(wts[:, n % 4, 0:w], take[:, s, 0:w], prod[:, s, 513 - w:513],
                                      ALU.mult).then_inc(sb_weights, 1)

                def own_heads(b, k):
                    dve.wait_ge(valued, b * NU + NU + (3 if k == DIL else NU))
                    if k == DIL:
                        dve.wait_ge(dil_weights, b + 1)
                        dve.reciprocal(top[:, 3:4], top[:, 2:3]).then_inc(inverted, 1)
                        dve.wait_ge(inverted, b + 1)
                        dve.scalar_tensor_tensor(out=o_own[:, k, :], in0=o_ps[:, :], scalar=top[:, 3:4],
                                                 in1=own[:, :], op0=ALU.mult, op1=ALU.mult).then_inc(owned, 1)
                    else:
                        dve.tensor_tensor(o_own[:, k, :], o_ps[:, :], own[:, :], ALU.mult).then_inc(owned, 1)

                with dve.Fori(0, B) as b:
                    queries(b)
                    keys_out(dve, kT, b, 0, copy, kT_out_v, 2)
                    for s in range(NU):
                        if s + 1 < NU:
                            keys_out(dve, kT, b, s + 1, copy, kT_out_v, 2)
                        if s == 7:
                            own_heads(b, DIL)
                        if kind[s] == DIL:
                            dilated(b, s)
                        else:
                            broken(b, s)
                    own_heads(b, SB)


class Semaphores:

    def __init__(self, nc, stack):
        self.nc, self.stack = nc, stack
        self.passed = self.sem("passed")

    def sem(self, name):
        return self.stack.enter_context(self.nc.semaphore(name))


def gains_stage(nc, cx, gains, ident_in, neg_in, ident, negc, ones):
    fetched, filled = cx.sem("gains_fetched"), cx.sem("gains_filled")
    with nc.Block() as block:
        @block.sync
        def _(sp):
            total = 0
            for dst, src in gains:
                sp.dma_start(dst, src.rearrange("(c p) -> p c", p=P), allow_slow_non_contiguous=True).then_inc(fetched, 16)
                total += 16
            sp.dma_start(ident[:, :], ident_in).then_inc(fetched, 16)
            sp.dma_start(negc[:, :], neg_in).then_inc(fetched, 16)
            sp.wait_ge(fetched, total + 32)

        @block.vector
        def _(dve):
            dve.memset(ones[:, :], 1.0).then_inc(filled, 1)
            dve.memset(cx.eps[:, :], EPS).then_inc(filled, 1)
            dve.wait_ge(filled, 2)


def decoder_step(nc, a, o):
    with ExitStack() as stack:
        cx = Semaphores(nc, stack)

        def sb(name, shape, dt=F32):
            return stack.enter_context(nc.sbuf_tensor(name, shape, dt))

        qkvT = nc.dram_tensor("qkvT", [6 * W, T], F32).ap()
        oT_dram = nc.dram_tensor("oT", [2 * W, T], F32).ap()
        by_distance = nc.dram_tensor("by_distance", [HEADS, LD], F32).ap()
        xT = sb("xT", [P, KC, T])
        ident, negc, ones = sb("ident", [P, P]), sb("negc", [P, P]), sb("ones", [P, P])
        cx.eps = sb("eps", [P, 1])
        g_attn, g_out, g_mlp, g_final = (sb(n, [P, KC]) for n in ("g_attn", "g_out", "g_mlp", "g_final"))
        y_p, y_s, sbk_p, sbv_p, sbk_s, sbv_s, wk_p, wv_p, wk_s, wv_s = o

        half = KC // 2
        gains_stage(nc, cx, [(g_attn[:, :], a["g_attn"][0]), (g_out[:, 0:half], a["g_out_sb"][0]),
                             (g_out[:, half:], a["g_out_dil"][0]), (g_mlp[:, :], a["g_mlp"][0]),
                             (g_final[:, :], a["g_final"])], a["ident"], a["neg_causal"], ident, negc, ones)
        load_tokens(nc, cx, a["x_prompt"], a["x_sample"], ident, xT)
        with ExitStack() as st:
            hi = st.enter_context(nc.sbuf_tensor("n1_hi", [P, KC, T], F32R))
            lo = st.enter_context(nc.sbuf_tensor("n1_lo", [P, KC, T], F32R))
            rms_stage(nc, cx, "n1", xT, g_attn, ones, 1, hi=hi, lo=lo)
            dense_stage(nc, cx, "qkv", a["w_in"][0], hi, lo, 6 * W // 512, store=qkvT)
        bias_stage(nc, cx, a["rel_bias"], a["one_hot"], a["ln_count"], by_distance)
        tails = [x[0, :, WIN - TS:WIN, :, :] for x in (wk_s, wv_s)]
        prompt_stage(nc, cx, qkvT, oT_dram, by_distance, a["sb_bias"], negc, ident,
                     [(sbk_p, sbk_s[0]), (sbv_p, sbv_s[0]), (wk_p, tails[0]), (wv_p, tails[1])])
        sample_stage(nc, cx, qkvT, oT_dram, by_distance, a["sb_bias"], a["page_table"],
                     (a["cache_sb_k"], a["cache_sb_v"]), (a["cache_win_k"], a["cache_win_v"]),
                     (tails[1], sbv_s[0]), a["neg_new"], a["own_head"], a["same_token"], ident)
        with ExitStack() as st:
            hi = st.enter_context(nc.sbuf_tensor("n2_hi", [P, KC, T], F32R))
            lo = st.enter_context(nc.sbuf_tensor("n2_lo", [P, KC, T], F32R))
            with nc.sbuf_tensor("o_all_T", [P, KC, T], F32) as o_in:
                rms_stage(nc, cx, "n2", o_in, g_out, ones, 2, hi=hi, lo=lo, load=oT_dram)
            dense_stage(nc, cx, "out", a["w_out"][0], hi, lo, D_MODEL // 512, residual=xT)
            rms_stage(nc, cx, "n3", xT, g_mlp, ones, 1, hi=hi, lo=lo)
            mlp_stage(nc, cx, a["w_up"][0], a["w_down"][0], hi, lo, xT,
                      [(a["cache_win_k"], wk_s), (a["cache_win_v"], wv_s)], cx.sem("window_moved"))
        with nc.sbuf_tensor("yT", [P, KC, T], F32) as yT:
            rms_stage(nc, cx, "n4", xT, g_final, ones, 1, plain=yT)
            store_tokens(nc, cx, yT, y_p, y_s, ident)


_INS = ['x_prompt', 'x_sample', 'cache_sb_k', 'cache_sb_v', 'cache_win_k', 'cache_win_v', 'page_table', 'rel_bias',
        'g_attn', 'w_in', 'sb_bias', 'g_out_sb', 'g_out_dil', 'w_out', 'g_mlp', 'w_up', 'w_down', 'g_final']
_HEAD = (HEADS, HD)
_OUTS = [(1, SEQ, D_MODEL), (B, TS, D_MODEL), (1, 1, SEQ) + _HEAD, (1, 1, SEQ) + _HEAD, (1, B, TS) + _HEAD,
         (1, B, TS) + _HEAD, (1, 1, SEQ) + _HEAD, (1, 1, SEQ) + _HEAD, (1, B, WIN) + _HEAD, (1, B, WIN) + _HEAD]


def shape_constants():
    import math
    import numpy as np
    big = np.float32(-1e30)
    dist = DIST0 - np.arange(LD)
    count = ((dist >= 0) & (dist <= 128)).astype(int) + ((dist >= 0) & (dist % 4 == 0) & (dist <= 512)) \
        + ((dist >= 0) & (dist % 16 == 0) & (dist <= 2048))
    d = np.maximum(dist, 1).astype(np.float32)
    exact, buckets = 16, 32
    large = exact + (np.log(d / exact) / math.log(WIN / exact) * (buckets - exact)).astype(np.int32)
    bucket = np.where(dist < exact, np.maximum(dist, 0), np.minimum(large, buckets - 1))
    one_hot = (np.arange(buckets)[:, None] == bucket[None, :]).astype(np.float32)
    ln_count = np.where(count > 0, np.log(np.maximum(count, 1)), big).astype(np.float32)
    row = np.arange(NS)
    return {
        "ident": np.eye(P, dtype=np.float32),
        "neg_causal": np.where(np.arange(P)[None, :] < np.arange(P)[:, None], 0, big).astype(np.float32),
        "one_hot": one_hot,
        "ln_count": np.ascontiguousarray(np.broadcast_to(ln_count, (HEADS, LD))),
        "neg_new": np.where(np.arange(TS)[None, :] < (row // HEADS)[:, None], 0, big).astype(np.float32),
        "own_head": (np.arange(W)[None, :] // HD == (row % HEADS)[:, None]).astype(np.float32),
        "same_token": (np.arange(TS)[None, :] == (row // HEADS)[:, None]).astype(np.float32),
    }


def kernel(**inputs):
    import numpy as _np
    import concourse.bacc as _bacc
    from concourse import mybir as _mybir
    from concourse.bass_utils import run_bass_kernel_spmd as _run

    nc = _bacc.Bacc("TRN2", target_bir_lowering=False, num_devices=1)
    arrays, args = {}, {}
    given = {name: _np.ascontiguousarray(inputs[name]) for name in _INS}
    for name, x in {**given, **shape_constants()}.items():
        arrays[f"in_{name}"] = x
        args[name] = nc.dram_tensor(f"in_{name}", x.shape, _mybir.dt.from_np(x.dtype), kind="ExternalInput").ap()
    outs = [nc.dram_tensor(f"out_{i}", shape, F32, kind="ExternalOutput").ap() for i, shape in enumerate(_OUTS)]
    decoder_step(nc, args, outs)
    r = _run(nc, [arrays], core_ids=[0])
    return tuple(r.results[0][f"out_{i}"] for i in range(len(_OUTS)))
```
